# Optimizing a Trainium2 kernel written in Bass

```python
import math
import jax, jax.numpy as jnp
from jax import lax
import numpy as np

D_MODEL = 1024
BATCH = 1
SEQ = 1024
DEPTH = 2
DEC_BATCH = 1
DEC_SEQ = 32
PAST_LEN = 256

CHUNK = 64
QBLOCK = 128
HEAD_DIM = 64
N_RET = 6
N_FOX = 6
N_DIFF = 6
DIFF_QK = HEAD_DIM // 2
RET_W = N_RET * HEAD_DIM
FOX_W = N_FOX * HEAD_DIM
DIFF_W = N_DIFF * HEAD_DIM
MIX_W = RET_W + FOX_W + DIFF_W
IN_W = 4 * RET_W + 3 * FOX_W + N_FOX + 3 * DIFF_W
D_FF = 4 * D_MODEL
ROPE_THETA = 10000.0
EPS = 1e-6
FORGET_BIAS = 3.0

kernel_name = 'hybrid_streaming_encoder_step'

def _split_points():
    sizes = [RET_W] * 4 + [FOX_W] * 3 + [N_FOX] + [DIFF_W] * 3
    return [int(s) for s in np.cumsum(sizes)[:-1]]

def _rmsnorm(x, g):
    xf = x.astype(jnp.float32)
    y = xf * lax.rsqrt(jnp.mean(xf * xf, axis=-1, keepdims=True) + EPS)
    return (y * g.astype(jnp.float32)).astype(x.dtype)

def _group_norm(x, g, b):
    B, L = x.shape[0], x.shape[1]
    xf = x.astype(jnp.float32)
    mu = jnp.mean(xf, axis=-1, keepdims=True)
    xc = xf - mu
    y = (xc * lax.rsqrt(jnp.mean(xc * xc, axis=-1, keepdims=True) + EPS)).reshape(B, L, -1)
    return (y * g.astype(jnp.float32) + b.astype(jnp.float32)).astype(x.dtype)

def _head_rmsnorm(x, g):
    B, L = x.shape[0], x.shape[1]
    xf = x.astype(jnp.float32)
    y = (xf * lax.rsqrt(jnp.mean(xf * xf, axis=-1, keepdims=True) + EPS)).reshape(B, L, -1)
    return (y * g.astype(jnp.float32)).astype(x.dtype)

def _rope(x, pos):
    half = x.shape[-1] // 2
    inv = ROPE_THETA ** (-jnp.arange(half, dtype=jnp.float32) / half)
    ang = pos.astype(jnp.float32)[:, None] * inv[None, :]
    shp = (1, x.shape[1]) + (1,) * (x.ndim - 3) + (half,)
    cos = jnp.cos(ang).reshape(shp)
    sin = jnp.sin(ang).reshape(shp)
    xf = x.astype(jnp.float32)
    x1, x2 = xf[..., :half], xf[..., half:]
    return jnp.concatenate([x1 * cos - x2 * sin, x1 * sin + x2 * cos], axis=-1).astype(x.dtype)

def _retention(q, k, v, s0):
    B, L, H, dk = q.shape
    C = min(CHUNK, L)
    n = L // C
    log_g = jnp.log1p(-jnp.exp2(-5.0 - jnp.arange(H, dtype=jnp.float32)))
    qc = q.astype(jnp.float32).reshape(B, n, C, H, dk)
    kc = k.astype(jnp.float32).reshape(B, n, C, H, dk) * (dk ** -0.5)
    vc = v.astype(jnp.float32).reshape(B, n, C, H, -1)
    idx = jnp.arange(C, dtype=jnp.float32)
    intra_decay = jnp.exp(log_g[:, None, None] * jnp.abs(idx[:, None] - idx[None, :]))
    scores = jnp.einsum('bnihd,bnjhd->bnhij', qc, kc) * intra_decay
    intra = jnp.einsum('bnhij,bnjhe->bnihe', scores, vc)
    k_w = jnp.exp((C - 1.0 - idx)[:, None] * log_g[None, :])
    u = jnp.einsum('bnjhd,bnjhe->nbhde', kc * k_w[:, :, None], vc)
    chunk_decay = jnp.exp(C * log_g)[:, None, None]

    def step(s, u_c):
        return chunk_decay * s + u_c, s

    s_last, s_before = lax.scan(step, s0.astype(jnp.float32), u)
    q_w = jnp.exp((idx + 1.0)[:, None] * log_g[None, :])
    cross = jnp.einsum('bnihd,nbhde->bnihe', qc * q_w[:, :, None], s_before)
    out = (intra + cross).reshape(B, L, H, -1)
    return out.astype(q.dtype), s_last

def _fox_attention(q, k, v, fq, fk, q_pos, k_pos):
    B, Lq, H, d = q.shape
    qb_len = min(QBLOCK, Lq)
    nb = Lq // qb_len
    scale = d ** -0.5
    q_blocks = q.reshape(B, nb, qb_len, H, d).transpose(1, 0, 2, 3, 4)
    f_blocks = fq.reshape(B, nb, qb_len, H).transpose(1, 0, 2, 3)
    p_blocks = q_pos.reshape(nb, qb_len)
    fk_t = jnp.transpose(fk, (0, 2, 1))[:, :, None, :]

    def block(args):
        qq, fqq, pq = args
        s = jnp.einsum('bqhd,bkhd->bhqk', qq, k, preferred_element_type=jnp.float32) * scale
        s = s + jnp.transpose(fqq, (0, 2, 1))[:, :, :, None] - fk_t
        mask = k_pos[None, :] <= pq[:, None]
        p = jax.nn.softmax(jnp.where(mask, s, -jnp.inf), axis=-1)
        return jnp.einsum('bhqk,bkhd->bqhd', p.astype(v.dtype), v)

    out = lax.map(block, (q_blocks, f_blocks, p_blocks))
    return out.transpose(1, 0, 2, 3, 4).reshape(B, Lq, H, d)

def _diff_attention(q, k, v, lam, q_pos, k_pos):
    B, Lq, H, _, dq = q.shape
    qb_len = min(QBLOCK, Lq)
    nb = Lq // qb_len
    scale = dq ** -0.5
    q_blocks = q.reshape(B, nb, qb_len, H, 2, dq).transpose(1, 0, 2, 3, 4, 5)
    p_blocks = q_pos.reshape(nb, qb_len)
    k_chunk = k_pos // CHUNK

    def block(args):
        qq, pq = args
        s = jnp.einsum('bqhcd,bkhcd->cbhqk', qq, k, preferred_element_type=jnp.float32) * scale
        mask = k_chunk[None, :] <= (pq // CHUNK)[:, None]
        p = jax.nn.softmax(jnp.where(mask, s, -jnp.inf), axis=-1)
        a = p[0] - lam * p[1]
        return jnp.einsum('bhqk,bkhd->bqhd', a.astype(v.dtype), v)

    out = lax.map(block, (q_blocks, p_blocks))
    return out.transpose(1, 0, 2, 3, 4).reshape(B, Lq, H, -1)

def _token_mixers(h, pos, k_pos, past, lam_init, w_in, b_forget, ret_norm_g, ret_norm_b,
                  lam_q1, lam_k1, lam_q2, lam_k2, diff_norm_g):
    B, L, _ = h.shape
    proj = h @ w_in
    rq, rk, rv, rg, fq, fk, fv, ff, dq, dk, dv = jnp.split(proj, _split_points(), axis=-1)
    rq = _rope(rq.reshape(B, L, N_RET, HEAD_DIM), pos)
    rk = _rope(rk.reshape(B, L, N_RET, HEAD_DIM), pos)
    rv = rv.reshape(B, L, N_RET, HEAD_DIM)
    fq = fq.reshape(B, L, N_FOX, HEAD_DIM)
    fk = fk.reshape(B, L, N_FOX, HEAD_DIM)
    fv = fv.reshape(B, L, N_FOX, HEAD_DIM)
    logf = jax.nn.log_sigmoid(ff.astype(jnp.float32) + b_forget.astype(jnp.float32))
    dq = _rope(dq.reshape(B, L, N_DIFF, 2, DIFF_QK), pos)
    dk = _rope(dk.reshape(B, L, N_DIFF, 2, DIFF_QK), pos).reshape(B, L, N_DIFF, HEAD_DIM)
    dv = dv.reshape(B, L, N_DIFF, HEAD_DIM)
    if past is None:
        s0 = jnp.zeros((B, N_RET, HEAD_DIM, HEAD_DIM), jnp.float32)
        fk_all, fv_all, logf_all, dk_all, dv_all = fk, fv, logf, dk, dv
    else:
        pfk, pfv, plogf, pdk, pdv, s0 = past
        fk_all = jnp.concatenate([pfk.astype(fk.dtype), fk], axis=1)
        fv_all = jnp.concatenate([pfv.astype(fv.dtype), fv], axis=1)
        logf_all = jnp.concatenate([plogf.astype(jnp.float32), logf], axis=1)
        dk_all = jnp.concatenate([pdk.astype(dk.dtype), dk], axis=1)
        dv_all = jnp.concatenate([pdv.astype(dv.dtype), dv], axis=1)
    r_out, s_new = _retention(rq, rk, rv, s0)
    r_out = jax.nn.silu(rg) * _group_norm(r_out, ret_norm_g, ret_norm_b)
    f_cum = jnp.cumsum(logf_all, axis=1)
    f_out = _fox_attention(fq, fk_all, fv_all, f_cum[:, -L:], f_cum, pos, k_pos)
    lq1, lk1 = lam_q1.astype(jnp.float32), lam_k1.astype(jnp.float32)
    lq2, lk2 = lam_q2.astype(jnp.float32), lam_k2.astype(jnp.float32)
    lam = jnp.exp(jnp.sum(lq1 * lk1)) - jnp.exp(jnp.sum(lq2 * lk2)) + lam_init
    d_out = _diff_attention(dq, dk_all.reshape(B, -1, N_DIFF, 2, DIFF_QK), dv_all, lam, pos, k_pos)
    d_out = _head_rmsnorm(d_out, diff_norm_g) * (1.0 - lam_init)
    mix = jnp.concatenate([r_out, f_out.reshape(B, L, FOX_W), d_out.astype(r_out.dtype)], axis=-1)
    return mix, (fk, fv, logf, dk, dv, s_new)

def _trunk_layer(x, c, pos, k_pos, past, lam_init, norm1_g, norm2_g, w_ada, b_ada, w_in, b_forget,
                 ret_norm_g, ret_norm_b, lam_q1, lam_k1, lam_q2, lam_k2, diff_norm_g, w_out, w_up, w_down):
    mod = jax.nn.silu(c) @ w_ada + b_ada
    sh1, sc1, g1, sh2, sc2, g2 = jnp.split(mod[:, None, :], 6, axis=-1)
    h = _rmsnorm(x, norm1_g) * (1.0 + sc1) + sh1
    mix, new_state = _token_mixers(h, pos, k_pos, past, lam_init, w_in, b_forget, ret_norm_g, ret_norm_b,
                                   lam_q1, lam_k1, lam_q2, lam_k2, diff_norm_g)
    x = x + g1 * (mix @ w_out)
    h = _rmsnorm(x, norm2_g) * (1.0 + sc2) + sh2
    x = x + g2 * (jnp.square(jax.nn.relu(h @ w_up)) @ w_down)
    return x, new_state

def setup_inputs(seed: int = 0) -> dict:
    key = jax.random.key(seed)
    ks = jax.random.split(key, 32)
    f32 = jnp.float32

    def nrm(k, shape, scale):
        return jax.random.normal(k, shape, f32) * scale

    return {
        'x_prompt': nrm(ks[0], (BATCH, SEQ, D_MODEL), 1.0),
        'x_sample': nrm(ks[1], (DEC_BATCH, DEC_SEQ, D_MODEL), 1.0),
        'cache_fox_k': nrm(ks[2], (DEPTH, DEC_BATCH, PAST_LEN, N_FOX, HEAD_DIM), 1.0),
        'cache_fox_v': nrm(ks[3], (DEPTH, DEC_BATCH, PAST_LEN, N_FOX, HEAD_DIM), 1.0),
        'cache_fox_logf': jax.nn.log_sigmoid(nrm(ks[4], (DEPTH, DEC_BATCH, PAST_LEN, N_FOX), 1.0) + FORGET_BIAS),
        'cache_diff_k': nrm(ks[5], (DEPTH, DEC_BATCH, PAST_LEN, N_DIFF, HEAD_DIM), 1.0),
        'cache_diff_v': nrm(ks[6], (DEPTH, DEC_BATCH, PAST_LEN, N_DIFF, HEAD_DIM), 1.0),
        'state_ret': nrm(ks[7], (DEPTH, DEC_BATCH, N_RET, HEAD_DIM, HEAD_DIM), 0.5),
        'c_prompt': nrm(ks[8], (BATCH, D_MODEL), 1.0),
        'c_sample': nrm(ks[9], (DEC_BATCH, D_MODEL), 1.0),
        'norm1_g': 1.0 + nrm(ks[10], (DEPTH, D_MODEL), 0.05),
        'norm2_g': 1.0 + nrm(ks[11], (DEPTH, D_MODEL), 0.05),
        'w_ada': nrm(ks[12], (DEPTH, D_MODEL, 6 * D_MODEL), D_MODEL ** -0.5),
        'b_ada': nrm(ks[13], (DEPTH, 6 * D_MODEL), 0.02),
        'w_in': nrm(ks[14], (DEPTH, D_MODEL, IN_W), D_MODEL ** -0.5),
        'b_forget': FORGET_BIAS + nrm(ks[15], (DEPTH, N_FOX), 0.1),
        'ret_norm_g': 1.0 + nrm(ks[16], (DEPTH, RET_W), 0.05),
        'ret_norm_b': nrm(ks[17], (DEPTH, RET_W), 0.02),
        'lam_q1': nrm(ks[18], (DEPTH, DIFF_QK), 0.1),
        'lam_k1': nrm(ks[19], (DEPTH, DIFF_QK), 0.1),
        'lam_q2': nrm(ks[20], (DEPTH, DIFF_QK), 0.1),
        'lam_k2': nrm(ks[21], (DEPTH, DIFF_QK), 0.1),
        'diff_norm_g': 1.0 + nrm(ks[22], (DEPTH, DIFF_W), 0.05),
        'w_out': nrm(ks[23], (DEPTH, MIX_W, D_MODEL), MIX_W ** -0.5),
        'w_up': nrm(ks[24], (DEPTH, D_MODEL, D_FF), D_MODEL ** -0.5),
        'w_down': nrm(ks[25], (DEPTH, D_FF, D_MODEL), D_FF ** -0.5),
        'final_g': 1.0 + nrm(ks[26], (D_MODEL,), 0.05),
    }

def reference(x_prompt, x_sample, cache_fox_k, cache_fox_v, cache_fox_logf, cache_diff_k, cache_diff_v,
              state_ret, c_prompt, c_sample, norm1_g, norm2_g, w_ada, b_ada, w_in, b_forget,
              ret_norm_g, ret_norm_b, lam_q1, lam_k1, lam_q2, lam_k2, diff_norm_g, w_out, w_up, w_down,
              final_g):
    lp = x_prompt.shape[1]
    ls = x_sample.shape[1]
    past_len = cache_fox_k.shape[2]
    p_pos = jnp.arange(lp, dtype=jnp.int32)
    s_pos = past_len + jnp.arange(ls, dtype=jnp.int32)
    s_kpos = jnp.arange(past_len + ls, dtype=jnp.int32)
    xp, xs = x_prompt, x_sample
    p_new, s_new = [], []
    for li in range(DEPTH):
        lam_init = 0.8 - 0.6 * math.exp(-0.3 * li)
        layer_w = (norm1_g[li], norm2_g[li], w_ada[li], b_ada[li], w_in[li], b_forget[li],
                   ret_norm_g[li], ret_norm_b[li], lam_q1[li], lam_k1[li], lam_q2[li], lam_k2[li],
                   diff_norm_g[li], w_out[li], w_up[li], w_down[li])
        xp, ps = _trunk_layer(xp, c_prompt, p_pos, p_pos, None, lam_init, *layer_w)
        past = (cache_fox_k[li], cache_fox_v[li], cache_fox_logf[li], cache_diff_k[li], cache_diff_v[li],
                state_ret[li])
        xs, ss = _trunk_layer(xs, c_sample, s_pos, s_kpos, past, lam_init, *layer_w)
        p_new.append(ps)
        s_new.append(ss)
    y_prompt = _rmsnorm(xp, final_g)
    y_sample = _rmsnorm(xs, final_g)
    p_fox_k = jnp.stack([s[0] for s in p_new])
    p_fox_v = jnp.stack([s[1] for s in p_new])
    p_fox_logf = jnp.stack([s[2] for s in p_new])
    p_diff_k = jnp.stack([s[3] for s in p_new])
    p_diff_v = jnp.stack([s[4] for s in p_new])
    p_ret_state = jnp.stack([s[5] for s in p_new])
    s_fox_k = jnp.stack([s[0] for s in s_new])
    s_fox_v = jnp.stack([s[1] for s in s_new])
    s_fox_logf = jnp.stack([s[2] for s in s_new])
    s_diff_k = jnp.stack([s[3] for s in s_new])
    s_diff_v = jnp.stack([s[4] for s in s_new])
    s_ret_state = jnp.stack([s[5] for s in s_new])
    return (y_prompt, y_sample, p_fox_k, p_fox_v, p_fox_logf, p_diff_k, p_diff_v, p_ret_state,
            s_fox_k, s_fox_v, s_fox_logf, s_diff_k, s_diff_v, s_ret_state)


_drawn_inputs = setup_inputs


def setup_inputs(seed=0):
    import zlib

    import numpy as np

    out = dict(_drawn_inputs(seed))
    spreads = {}
    factors = {'cache_fox_logf': 12.008,
     'ret_norm_g': 3.54,
     'ret_norm_b': 8.0,
     'lam_q1': 3.147,
     'lam_q2': 2.898,
     'lam_k2': 5.83,
     'diff_norm_g': 2.706}
    for name, (base, spread) in spreads.items():
        noise = np.random.default_rng([zlib.crc32(name.encode()), seed]).standard_normal(out[name].shape)
        drawn = base * np.exp(spread * noise) if base else spread * noise
        out[name] = __import__('jax').numpy.asarray(drawn.astype(out[name].dtype))
    for name, factor in factors.items():
        out[name] = (out[name] * factor).astype(out[name].dtype)
    return out
```

```python
import numpy as np
import concourse.bass as bass
import concourse.mybir as mybir

D, FF, L = 1024, 4096, 2
TP, TS, PAST, CHUNK = 1024, 32, 256, 64
T = TP + TS
KB = D // 128
HD, PAIRS = 64, 3
GW = 352
GROUPS = T // GW
QT = 9
NKEY = T + PAST
UNIT = 1024
UNITS = [4, 3, 3]
OUT_UNITS = 4
MLP_CHUNKS, FB = 8, 4
PAIR_BASE = [0, 16, 29]
OUT_BASE = [12, 25, 38]
MLP_BASE = 42
NU = MLP_BASE + 8 * MLP_CHUNKS
ADA_UNITS, ADA_SLOTS = 48, 6
EPS = 1e-6
NEG = -1e30
PHASES = 11
PRIME = 3


def rows(t):
    return 128 if t < 8 else TS


def segments(g):
    a, b = g * GW, (g + 1) * GW
    if b <= TP:
        return [(a, b, 0)]
    return [(a, TP, 0), (TP, b, 1)]


def key_tiles(t):
    if t < 8:
        return [(128 * i, 128, i) for i in range(t + 1)]
    return [(TP, TS, 8), (T, 128, 9), (T + 128, 128, 10)]


def key_groups(t):
    k = key_tiles(t)
    return [k[i:i + 4] for i in range(0, len(k), 4)]


class Chain:

    def __init__(self, eng, sem):
        self.eng, self.sem, self.k = eng, sem, 0

    def mark(self, ins):
        ins.then_inc(self.sem, 1)
        self.k += 1
        return self.k

    def link(self, ins):
        self.eng.wait_ge(self.sem, self.mark(ins))

    def wait(self, k):
        self.eng.wait_ge(self.sem, k)

    def restart(self, settle):
        if self.k:
            self.eng.wait_ge(self.sem, self.k)
            settle(self.eng)
            self.eng.sem_clear(self.sem)
            self.k = 0


def build(nc, I, O):
    F32, F32R, BF = mybir.dt.float32, mybir.dt.float32r, mybir.dt.bfloat16
    ALU, ACT, AX = mybir.AluOpType, mybir.ActivationFunctionType, mybir.AxisListType
    ds = bass.ds

    place = [(nc.sbuf_base + 31) // 32 * 32]

    def at(name, shape, dt, offset=None):
        size = int(np.prod(shape[1:])) * (2 if dt == BF else 4)
        here = place[0] if offset is None else offset
        if offset is None:
            place[0] += (size + 31) // 32 * 32
        assert here + size <= nc.sbuf_usable_end, (name, here + size)
        return nc.alloc_sbuf_tensor_at(name, list(shape), dt, offset=here), here + (size + 31) // 32 * 32

    def sb(name, shape, dt=F32):
        return at(name, shape, dt)[0]

    x = sb("x", [128, KB * T])
    h_hi = sb("h_hi", [128, KB * T], F32R)
    h_lo = sb("h_lo", [128, KB * T], F32R)
    w_hi = sb("w_hi", [128, 3, UNIT], F32R)
    w_lo = sb("w_lo", [128, 3, UNIT], F32R)
    raw = sb("raw", [128, 2, UNIT])
    ident = sb("ident", [128, 128])
    mean_of = sb("mean_of", [128, 128])
    ident_bf = sb("ident_bf", [128, 128], BF)
    mask_bf = sb("mask_bf", [128, 2, 128], BF)
    sel = sb("sel", [128, 6, 128], BF)
    sel_pair = sb("sel_pair", [128, 2, 128], BF)
    rope_r = sb("rope_r", [128, QT, 2, 32])
    rope_d = sb("rope_d", [128, QT, 2, 16])
    kw_t = sb("kw_t", [128, 2, 6])
    qw_t = sb("qw_t", [128, 6])
    cd_t = sb("cd_t", [128, 2, 3])
    consts = sb("consts", [128, 4])
    cond = sb("cond", [128, KB, 2])
    cond_e = sb("cond_e", [128, KB, 2])
    mod_row = sb("mod_row", [2, 512])
    mod = sb("mod", [128, 48, 2])
    ada_bias = sb("ada_bias", [128, 48])
    norm_g = sb("norm_g", [128, 2, KB])
    scale_in = sb("scale_in", [128, 2, KB, 2])
    final_g = sb("final_g", [128, KB])
    vec = sb("vec", [128, 3, 3])
    bias_f = sb("bias_f", [6, 1])
    lam_v = sb("lam_v", [128, 4, 32])
    lam_p = sb("lam_p", [128, 32])
    lam_c = sb("lam_c", [128, 2])
    lam_s = sb("lam_s", [128, 2])
    lam_e = sb("lam_e", [128, 2])
    lam_n = sb("lam_n", [128, 1])
    nm = sb("nm", [128, 4])
    rs = sb("rs", [128, 4])
    ri = sb("ri", [128, 2])
    coef = sb("coef", [128, 1])
    st1 = sb("st1", [128, 18])
    st2 = sb("st2", [128, 18])
    st3 = sb("st3", [128, 18])

    region_a = place[0]
    mix_hi, e = at("mix_hi", [128, PAIRS * T], F32R, region_a)
    mix_lo, region_b = at("mix_lo", [128, PAIRS * T], F32R, e)
    act_hi, e = at("act_hi", [128, FB * T], F32R, region_a)
    act_lo, e = at("act_lo", [128, FB * T], F32R, e)
    relu_b, e = at("relu_b", [128, 2, GW], F32, e)
    sq_b, mlp_end = at("sq_b", [128, 2, GW], F32, e)
    ada_w, _ = at("ada_w", [128, ADA_SLOTS, UNIT], F32, mlp_end)
    sq, e = at("sq", [128, 2, GW], F32, region_b)
    tn, e = at("tn", [128, 2, GW], F32, e)
    rb, e = at("rb", [128, 2, GW], F32, e)
    assert e <= mlp_end
    kT, e = at("kT", [128, NKEY], F32, region_b)
    qT, e = at("qT", [128, T], F32, e)
    v_tok, e = at("v_tok", [128, 11, 128], F32, e)
    qk_tok, e = at("qk_tok", [128, 2, 256], F32, e)
    o_tok, e = at("o_tok", [128, QT, 128], F32, e)
    own = e
    gate, e = at("gate", [128, T], F32, own)
    states, e = at("states", [128, 19, HD], F32, e)
    s_mix, e = at("s_mix", [128, 2, 128], F32, e)
    decay, e = at("decay", [128, 2, 128], F32, e)
    sq_r, _ = at("sq_r", [128, QT * 128], F32, e)
    rope_r_tmp, _ = at("rope_r_tmp", [128, 512], F32, e)
    prob, e = at("prob", [128, 2, 1024], F32, own)
    sq_d, _ = at("sq_d", [128, QT * 128], F32, own)
    rope_d_tmp, _ = at("rope_d_tmp", [128, 512], F32, own)
    pT, e = at("pT", [128, 2, 4, 128], F32, e)
    cum_bf, _ = at("cum_bf", [128, NKEY], BF, e)
    fz, e = at("fz", [6, T], F32, region_b)
    fe, e = at("fe", [6, T], F32, e)
    cum, e = at("cum", [6, NKEY], F32, e)
    cum_mid, e = at("cum_mid", [6, NKEY], BF, e)
    tri, e = at("tri", [128, 128 + 512], F32, e)
    lf_tok, e = at("lf_tok", [128, 11, 6], F32, e)
    wf_raw, e = at("wf_raw", [128, 176], F32, e)
    wf_hi, e = at("wf_hi", [128, 176], F32R, e)
    wf_lo, e = at("wf_lo", [128, 176], F32R, e)
    assert e <= own + 8192 + 4096
    ps = nc.alloc_psum_tensor("ps", [128, 8, 512], F32)
    psf = ps[:].rearrange("p b c -> p (b c)")

    def S(name):
        return nc.alloc_semaphore(name)

    passed, const_in, layer_in, act_self, dve_self, pool_hi = S("passed"), S("const_in"), S("layer_in"), S("act_self"), S("dve_self"), S("pool_hi")
    act_done, dve_done = S("act_done"), S("dve_done")
    ada_in = [S(f"ada_in{i}") for i in range(ADA_SLOTS)]
    raw_in = [S("raw_in0"), S("raw_in1")]
    ada_used, raw_used, w_ready, w_used = S("ada_used"), S("raw_used"), S("w_ready"), S("w_used")
    cond_exp, cond_ready = S("cond_exp"), S("cond_ready")
    mod_ps, mod_rowed, mod_turned, mod_kept = S("mod_ps"), S("mod_rowed"), S("mod_turned"), S("mod_kept")
    lam_dot, lam_exp = S("lam_dot"), S("lam_exp")
    sq_ready, sq_used, ms_ready, rb_ready, tn_ready, hi_ready, lo_ready = [
        S(n) for n in ("sq_ready", "sq_used", "ms_ready", "rb_ready", "tn_ready", "hi_ready", "lo_ready")]
    up_ps, up_relu, up_hi, up_lo, down_ps, down_kept, sq_kept = [
        S(n) for n in ("up_ps", "up_relu", "up_hi", "up_lo", "down_ps", "down_kept", "sq_kept")]
    out_ps, out_kept = S("out_ps"), S("out_kept")
    y_ready, y_out = S("y_ready"), S("y_out")
    f_ps, f_exp, f_ln, f_z, f_log, f_turned, f_tok, f_cum, f_rows, f_wsplit, f_in, f_cache, f_out = [
        S(n) for n in ("f_ps", "f_exp", "f_ln", "f_z", "f_log", "f_turned", "f_tok", "f_cum", "f_rows", "f_wsplit", "f_in",
                       "f_cache", "f_out")]
    M = []
    for m in range(3):
        names = ["proj", "qk_kept", "v_kept", "turned", "qkT_kept", "o_ps", "o_kept", "stat", "rstd", "normed",
                 "mix_turned", "mix_hi_kept", "mix_lo_kept", "kv_out", "cache_k", "cache_v"]
        names += [["u_ps", "state_kept", "s_ps", "s_kept", "gate_ps", "gate_exp", "gate_kept", "y_pre", "y_gated",
                   "decay_in", "state_in", "state_out"],
                  ["score", "row_max", "exped", "p_turned", "pT_even", "pT_odd", "pv", "sel_kept"],
                  ["score", "row_max", "exped", "p_turned", "pT_even", "pT_odd", "pv", "combined"]][m]
        M.append({n: S(f"m{m}_{n}") for n in names})

    def keep_turned(eng, copy, s, n, i, g, tiles, done):
        r = rows(i // 2)
        eng.wait_ge(s["p_turned"], n * 26 + (g + 1))
        if g >= 2:
            eng.wait_ge(s["pv"], n * 26 + (g - 1))
        src = ps[:, 4 + g % 2, :].rearrange("p (y c) -> p y c", y=4)
        first = 0
        if tiles[0][1] < 128:
            copy(pT[0:TS, g % 2, 0, 0:r], src[0:TS, 0, 0:r])
            first = 1
        copy(pT[:, g % 2, first:len(tiles), 0:r], src[:, first:len(tiles), 0:r]).then_inc(s[done], 1)

    CONSTS = [(ident[:], "c_ident"), (mean_of[:], "c_mean"), (ident_bf[:], "c_ident_bf"), (mask_bf[:], "c_mask"),
              (sel[:], "c_sel"), (rope_r[:], "c_rope_r"), (rope_d[:], "c_rope_d"), (kw_t[:], "c_kw"), (qw_t[:], "c_qw"),
              (cd_t[:], "c_cd"), (consts[:], "c_consts"), (final_g[:], "final_g"), (x[:], "x"), (cond[:], "c")]
    LAYER = [(ada_bias[:], "b_ada"), (norm_g[:], "norm_g"), (vec[:], "vec"), (bias_f[:], "b_forget"), (lam_v[:], "lam"),
             (lam_c[:], "c_lam")]

    def settle(e):
        e.sem_inc(passed, 1)

    def from_layer(name, li):
        src = I[name][ds(li, 1)]
        dims = "abcdef"[:len(src.shape) - 1]
        return src.rearrange(f"o {' '.join(dims)} -> (o {dims[0]}) {' '.join(dims[1:])}")

    def pair_ap(a, n):
        src = a[ds(n, 1)]
        dims = "abcdef"[:len(src.shape) - 1]
        return src.rearrange(f"o {' '.join(dims)} -> (o {dims[0]}) {' '.join(dims[1:])}")

    def begin(e, li, p):
        e.wait_ge(act_done, li * PHASES + (p + PRIME))
        e.wait_ge(dve_done, li * PHASES + (p + PRIME))

    def proj_operands(slot, c, hi_w, hi_h):
        return (w_hi if hi_w else w_lo), (h_hi if hi_h else h_lo)

    PASSES = [(w_hi, 0), (w_lo, 0), (w_hi, 1)]

    with nc.Block() as block:

        @block.sync
        def _(sp):
            with sp.Fori(0, L) as li:
                sp.wait_ge(act_done, li * PHASES + (PRIME - 2))
                sp.wait_ge(dve_done, li * PHASES + (PRIME - 2))
                settle(sp)
                with sp.Fori(0, ADA_UNITS // ADA_SLOTS) as r:
                    for s in range(ADA_SLOTS):
                        sp.wait_ge(ada_used, li * ADA_UNITS + r * ADA_SLOTS + (s - ADA_SLOTS + 1 + ADA_SLOTS))
                        sp.dma_start(ada_w[:, s, :], I["w_ada"][ds(li * ADA_UNITS + r * ADA_SLOTS + s, 1)].rearrange(
                            "o p c -> (o p) c")).then_inc(ada_in[s], 16)
                settle(sp)
                with sp.Fori(0, NU // 2) as r:
                    for s in range(2):
                        sp.wait_ge(raw_used, li * NU + r * 2 + (s - 1 + PRIME - 1))
                        sp.dma_start(raw[:, s, :], I["w"][ds(li * NU + r * 2 + s, 1)].rearrange(
                            "o p c -> (o p) c")).then_inc(raw_in[s], 16)

        @block.gpsimd
        def _(pool):
            pool.sem_inc(raw_used, PRIME - 1)

            def split(li, u, uc, slot, width, used):
                pool.wait_ge(raw_in[uc % 2], (li * (NU // 2) + (u - uc % 2) // 2 + 1 if isinstance(u, int) else u) * 16)
                pool.wait_ge(w_used, used)
                settle(pool)
                pool.tensor_copy(w_hi[:, slot, 0:width], raw[:, uc % 2, 0:width]).then_inc(pool_hi, 1)
                pool.wait_ge(pool_hi, 1)
                pool.sem_clear(pool_hi)
                pool.tensor_tensor(w_lo[:, slot, 0:width], raw[:, uc % 2, 0:width], w_hi[:, slot, 0:width].bitcast(F32),
                                   ALU.subtract).then_inc(w_ready, 1)
                pool.wait_ge(w_ready, li * NU + u + 1 if isinstance(u, int) else used_after[0])
                pool.sem_inc(raw_used, 1)

            used_after = [None]
            with pool.Fori(0, L) as li:
                slots = []
                for m in range(3):
                    slots += [0, 1, 2, 0][:UNITS[m]] * PAIRS + [0, 1] * (OUT_UNITS // 2)
                for u, slot in enumerate(slots):
                    before = [v for v in range(u) if slots[v] == slot]
                    last = before[-1] + 1 if before else 0
                    split(li, u, u, slot, UNIT, li * NU + (last + 1))
                settle(pool)
                with pool.Fori(0, 4 * MLP_CHUNKS) as r:
                    for s in range(2):
                        used_after[0] = li * NU + r * 2 + (MLP_BASE + s + 1)
                        split(li, li * (NU // 2) + r + (MLP_BASE // 2 + 1), s, s, UNIT,
                              li * NU + r * 2 + (MLP_BASE + s - 1 + 1))

        @block.tensor
        def _(pe):
            mm = nc.tensor.matmul
            turn = nc.tensor.transpose
            pe.sem_inc(ada_used, ADA_SLOTS)
            pe.sem_inc(w_used, 1)
            pe.sem_inc(mod_turned, 1)
            pe.sem_inc(sq_used, 2)
            pe.wait_ge(const_in, 16 * len(CONSTS))
            pe.wait_ge(cond_ready, 1)

            def ada(li):
                begin(pe, li, 0)
                settle(pe)
                with pe.Fori(0, ADA_UNITS // (2 * ADA_SLOTS)) as r:
                    for q in range(3):
                        n = li * 12 + r * 3 + q
                        pe.wait_ge(mod_rowed, n + 1)
                        for i in range(4):
                            s = (q * 4 + i) % ADA_SLOTS
                            pe.wait_ge(ada_in[s], (li * 8 + r * 2 + ((q * 4 + i) // ADA_SLOTS + 1)) * 16)
                            for k in range(2):
                                last = mm(ps[0:2, 0, :], cond[:, 2 * i + k, :], ada_w[:, s, k * 512:(k + 1) * 512],
                                          start=(i + k == 0), stop=(i == 3 and k == 1))
                            last.then_inc(ada_used, 1)
                        pe.wait_ge(ada_used, li * ADA_UNITS + r * 12 + (q * 4 + 4 + ADA_SLOTS))
                        pe.sem_inc(mod_ps, 1)
                        pe.wait_ge(mod_rowed, n + 2)
                        pe.wait_ge(mod_kept, n + 1)
                        settle(pe)
                        for b in range(4):
                            last = mm(ps[:, 1, 2 * b:2 * b + 2], mod_row[:, b * 128:(b + 1) * 128], ident[0:2, 0:2],
                                      start=True, stop=True)
                        last.then_inc(mod_turned, 1)

            def norm(li, c):
                for g in range(GROUPS):
                    for k in range(KB):
                        pe.wait_ge(sq_ready, c * 24 + (g * KB + k + 1))
                        last = mm(ps[:, g, 0:GW], mean_of[:], sq[:, k % 2, :], start=(k == 0), stop=(k == KB - 1))
                        last.then_inc(sq_used, 1)
                    pe.wait_ge(sq_used, c * 24 + (g * KB + KB + 2))
                    pe.sem_inc(ms_ready, 1)

            def pairs(m, li):
                s = M[m]
                NC = 2 if m == 2 else 1
                NA = 18 * NC
                begin(pe, li, [2, 5, 7][m])
                settle(pe)
                with pe.Fori(0, PAIRS) as j:
                    n = li * PAIRS + j
                    ub = li * NU + j * UNITS[m] + PAIR_BASE[m]

                    def turn_qk(t):
                        r, bank = rows(t), 4 + t % 2
                        if t == 0:
                            pe.wait_ge(s["mix_hi_kept"], n * 3 + 1)
                            pe.wait_ge(s["mix_lo_kept"], n * 3 + 1)
                        if t >= 2:
                            pe.wait_ge(s["qkT_kept"], n * 9 + (t - 1))
                        pe.wait_ge(s["qk_kept"], n * 9 + (t + 1))
                        if r < 128:
                            settle(pe)
                        turn(ps[:, bank, 0:r], qk_tok[0:r, t % 2, 0:128], ident[0:r, 0:r])
                        turn(ps[:, bank, 128:128 + r], qk_tok[0:r, t % 2, 128:256], ident[0:r, 0:r]).then_inc(s["turned"], 1)

                    pe.wait_ge(w_ready, ub + 3)
                    for t in range(QT):
                        if t >= 2:
                            pe.wait_ge(s["qk_kept"], n * 9 + (t - 1))
                            pe.wait_ge(s["v_kept"], n * 9 + (t - 1))
                        r = rows(t)
                        for k in range(KB):
                            for w, low in PASSES:
                                last = mm(ps[0:r, 6 + t % 2, 0:384], (h_lo if low else h_hi)[:, k * T + 128 * t:k * T + 128 * t + r],
                                          w[:, :, k * 128:(k + 1) * 128],
                                          start=(k == 0 and w is w_hi and not low), stop=(k == KB - 1 and low == 1))
                        last.then_inc(s["proj"], 1)
                        if t:
                            turn_qk(t - 1)
                    pe.wait_ge(s["proj"], n * 9 + 9)
                    pe.sem_inc(w_used, 3)
                    turn_qk(8)
                    pe.wait_ge(s["qkT_kept"], n * 9 + 9)
                    pe.wait_ge(s["v_kept"], n * 9 + 9)
                    settle(pe)
                    if m == 0:
                        retention(s, n, ub)
                    else:
                        attention(m, s, n, NC, NA)
                    for i, bank in enumerate((4, 5, 3)):
                        pe.wait_ge(s["normed"], n + 1)
                        settle(pe)
                        for t in range(4 * i, min(4 * i + 4, QT)):
                            r = rows(t)
                            last = turn(ps[:, bank, 128 * (t % 4):128 * (t % 4) + r], o_tok[0:r, t, :], ident[0:r, 0:r])
                        last.then_inc(s["mix_turned"], 1)

            def retention(s, n, ub):
                for t in range(8):
                    for cp in range(2):
                        for h in range(2):
                            mm(ps[64 * h:64 * h + 64, cp, 64 * t:64 * t + 64], o_tok[64 * cp:64 * cp + 64, t, 64 * h:64 * h + 64],
                               v_tok[64 * cp:64 * cp + 64, t, 64 * h:64 * h + 64], start=True, stop=True)
                for h in range(2):
                    last = mm(ps[64 * h:64 * h + 64, 2, 0:64], o_tok[0:TS, 8, 64 * h:64 * h + 64],
                              v_tok[0:TS, 8, 64 * h:64 * h + 64], start=True, stop=True)
                last.then_inc(s["u_ps"], 1)

                def scores(i):
                    t, h = divmod(i, 2)
                    r = rows(t)
                    if i >= 2:
                        pe.wait_ge(s["s_kept"], n * 18 + (i - 1))
                    settle(pe)
                    mm(ps[0:r, 4 + i % 2, 0:r], kT[64 * h:64 * h + 64, 128 * t:128 * t + r],
                       qT[64 * h:64 * h + 64, 128 * t:128 * t + r], start=True, stop=True).then_inc(s["s_ps"], 1)

                scores(0)
                for i in range(18):
                    t, h = divmod(i, 2)
                    r = rows(t)
                    if i + 1 < 18:
                        scores(i + 1)
                    if i == 0:
                        pe.wait_ge(s["state_kept"], n + 1)
                    if i >= 2:
                        pe.wait_ge(s["o_kept"], n * 18 + (i - 1))
                    pe.wait_ge(s["s_kept"], n * 18 + (i + 1))
                    bank = 6 + i % 2
                    if r < 128:
                        settle(pe)
                    mm(ps[0:r, bank, 0:64], s_mix[0:r, i % 2, 0:r], v_tok[0:r, t, 64 * h:64 * h + 64], start=True,
                       stop=False, skip_group_check=True)
                    for cp in range(2 if t < 8 else 1):
                        w = 64 if t < 8 else TS
                        last = mm(ps[64 * cp:64 * cp + w, bank, 0:64],
                                  qT[64 * h:64 * h + 64, 128 * t + 64 * cp:128 * t + 64 * cp + w],
                                  states[64 * h:64 * h + 64, 2 * t + cp if t < 8 else 17, :], start=False, stop=True,
                                  skip_group_check=True)
                    last.then_inc(s["o_ps"], 1)
                pe.wait_ge(w_ready, ub + 4)
                for g in range(GROUPS):
                    for k in range(KB):
                        for w, low in PASSES:
                            last = mm(ps[:, g, 0:GW], w[:, 0, k * 128:(k + 1) * 128],
                                      (h_lo if low else h_hi)[:, k * T + g * GW:k * T + (g + 1) * GW],
                                      start=(k == 0 and w is w_hi and not low), stop=(k == KB - 1 and low == 1))
                    last.then_inc(s["gate_ps"], 1)
                pe.wait_ge(s["gate_ps"], n * 3 + 3)
                pe.sem_inc(w_used, 1)

            def attention(m, s, n, NC, NA):
                K = HD // NC
                pe.wait_ge(s["cache_k"], (n + 1) * 16)
                pe.wait_ge(s["cache_v"], (n + 1) * 16)
                if m == 1:
                    pe.wait_ge(s["sel_kept"], n + 1)

                def score(i):
                    t, h = divmod(i, 2)
                    r = rows(t)
                    k0, nk = (0, 128 * (t + 1)) if t < 8 else (TP, TS + PAST)
                    for c in range(NC):
                        a = i * NC + c
                        if a >= 2:
                            pe.wait_ge(s["exped"], n * NA + (a - 1))
                        settle(pe)
                        p0 = 64 * h + K * c
                        for b in range((nk + 511) // 512):
                            w = min(512, nk - 512 * b)
                            out = ps[0:r, 2 * (a % 2) + b, 0:w]
                            diagonal = (t // 4 == b and t < 8) or (t == 8 and m == 1)
                            last = mm(out, qT[p0:p0 + K, 128 * t:128 * t + r], kT[p0:p0 + K, k0 + 512 * b:k0 + 512 * b + w],
                                      start=True, stop=(m == 2 and not diagonal), skip_group_check=True)
                            if m == 1:
                                last = mm(out, sel_pair[0:96, h, 0:r], cum_bf[0:96, k0 + 512 * b:k0 + 512 * b + w],
                                          start=False, stop=not diagonal, skip_group_check=True)
                            if diagonal:
                                d0 = 128 * (t % 4) if t < 8 else 0
                                last = mm(ps[0:r, 2 * (a % 2) + b, d0:d0 + r], ident_bf[0:r, 0:r], mask_bf[0:r, m - 1, 0:r],
                                          start=False, stop=True, skip_group_check=True)
                        last.then_inc(s["score"], 1)

                gi = [0]

                def weigh(i):
                    t, h = divmod(i, 2)
                    r = rows(t)
                    groups = key_groups(t)
                    if m == 1:
                        pe.wait_ge(s["exped"], n * NA + (i + 1))
                    else:
                        pe.wait_ge(s["combined"], n * 18 + (i + 1))
                    g0 = gi[0]
                    for q, tiles in enumerate(groups):
                        g = g0 + q
                        if g >= 2:
                            pe.wait_ge(s[["pT_even", "pT_odd"][g % 2]], n * 13 + g // 2)
                        if r < 128:
                            settle(pe)
                        for y, (k0, kr, vt) in enumerate(tiles):
                            c0 = k0 if t < 8 else k0 - TP
                            last = turn(ps[0:kr, 4 + g % 2, 128 * y:128 * y + r],
                                        prob[0:r, (i % 2 if m == 1 else 0), c0:c0 + kr], ident[0:r, 0:r])
                        last.then_inc(s["p_turned"], 1)
                    if i >= 2:
                        pe.wait_ge(s["o_kept"], n * 18 + (i - 1))
                    for q, tiles in enumerate(groups):
                        g = g0 + q
                        pe.wait_ge(s[["pT_even", "pT_odd"][g % 2]], n * 13 + (g // 2 + 1))
                        if r < 128:
                            settle(pe)
                        for y, (k0, kr, vt) in enumerate(tiles):
                            last = mm(ps[0:r, 6 + i % 2, 0:64], pT[0:kr, g % 2, y, 0:r], v_tok[0:kr, vt, 64 * h:64 * h + 64],
                                      start=(q == 0 and y == 0), stop=(q == len(groups) - 1 and y == len(tiles) - 1))
                        last.then_inc(s["pv"], 1)
                    gi[0] += len(groups)

                score(0)
                for i in range(18):
                    if i + 1 < 18:
                        score(i + 1)
                    weigh(i)

            def out_proj(m, li):
                begin(pe, li, [3, 6, 8][m])
                c = li * 3 + m
                settle(pe)
                with pe.Fori(0, 2) as r:
                    for s in range(2):
                        pe.wait_ge(w_ready, li * NU + r * 2 + (OUT_BASE[m] + s + 1))
                        for o in range(2):
                            for g in range(GROUPS):
                                i = (s * 2 + o) * 3 + g
                                pe.wait_ge(out_kept, c * 24 + r * 12 + (i - 6 + 1 + 6))
                                for k in range(3):
                                    for w, low in PASSES:
                                        last = mm(ps[:, i % 6, 0:GW], w[:, s, k * 256 + o * 128:k * 256 + o * 128 + 128],
                                                  (mix_lo if low else mix_hi)[:, k * T + g * GW:k * T + (g + 1) * GW],
                                                  start=(k == 0 and w is w_hi and not low), stop=(k == 2 and low == 1))
                                last.then_inc(out_ps, 1)
                        pe.wait_ge(out_ps, c * 24 + r * 12 + ((s * 2 + 2) * 3))
                        pe.sem_inc(w_used, 1)

            def forget(li):
                begin(pe, li, 4)
                pe.wait_ge(f_wsplit, li + 1)
                for g in range(GROUPS):
                    for k in range(KB):
                        for w, low in ((wf_hi, 0), (wf_lo, 0), (wf_hi, 1)):
                            last = mm(ps[:, g, 0:GW], w[:, 6 * k:6 * k + 128],
                                      (h_lo if low else h_hi)[:, k * T + g * GW:k * T + (g + 1) * GW],
                                      start=(k == 0 and w is wf_hi and not low), stop=(k == KB - 1 and low == 1))
                last.then_inc(f_ps, 1)
                pe.wait_ge(f_log, li + 1)
                settle(pe)
                for t in range(QT):
                    r = rows(t)
                    last = turn(ps[0:r, 3, 8 * t:8 * t + 6], fz[:, 128 * t:128 * t + r], ident[0:6, 0:6])
                last.then_inc(f_turned, 1)
                pe.wait_ge(f_tok, li + 1)
                pe.wait_ge(f_in, (li + 1) * 48)
                for b in range(2):
                    for t in range(4 * b + 4):
                        c0 = max(128 * t, 512 * b)
                        w = 512 * (b + 1) - c0
                        u0 = 0 if 128 * t >= 512 * b else 128
                        mm(ps[0:6, 4 + b, c0 - 512 * b:512], lf_tok[:, t, :], tri[:, u0:u0 + w], start=(t == 0),
                           stop=(t == 4 * b + 3), skip_group_check=True)
                mm(ps[0:6, 6, 0:288], lf_tok[:, 9, :], tri[:, 0:288], start=True, stop=False, skip_group_check=True)
                mm(ps[0:6, 6, 128:288], lf_tok[:, 10, :], tri[:, 0:160], start=False, stop=False, skip_group_check=True)
                mm(ps[0:6, 6, 256:288], lf_tok[0:TS, 8, :], tri[0:TS, 0:TS], start=False, stop=True,
                   skip_group_check=True).then_inc(f_cum, 1)

            def mlp(li):
                begin(pe, li, 10)
                settle(pe)
                with pe.Fori(0, MLP_CHUNKS) as f:
                    n = li * MLP_CHUNKS + f
                    ub = li * NU + f * 8 + MLP_BASE
                    for b in range(FB):
                        pe.wait_ge(w_ready, ub + (b + 1))
                        for g in range(GROUPS):
                            i = b * 3 + g
                            if i < 6:
                                pe.wait_ge(down_kept, n * 24 + (i - 6 + 1 + 6))
                            else:
                                pe.wait_ge(up_relu, n * 12 + (i - 6 + 1))
                            for k in range(KB):
                                for w, low in PASSES:
                                    last = mm(ps[:, i % 6, 0:GW], w[:, b % 2, k * 128:(k + 1) * 128],
                                              (h_lo if low else h_hi)[:, k * T + g * GW:k * T + (g + 1) * GW],
                                              start=(k == 0 and w is w_hi and not low), stop=(k == KB - 1 and low == 1))
                            last.then_inc(up_ps, 1)
                        pe.wait_ge(up_ps, n * 12 + (b * 3 + 3))
                        pe.sem_inc(w_used, 1)
                    for b in range(4):
                        pe.wait_ge(w_ready, ub + (b + 5))
                        for o in range(2):
                            for g in range(GROUPS):
                                i = (b * 2 + o) * 3 + g
                                if i < 6:
                                    pe.wait_ge(up_relu, n * 12 + (i + 7))
                                else:
                                    pe.wait_ge(down_kept, n * 24 + (i - 6 + 1 + 6))
                                if i == 0:
                                    pe.wait_ge(up_lo, n * 12 + 13)
                                for k in range(FB):
                                    for w, low in PASSES:
                                        last = mm(ps[:, i % 6, 0:GW], w[:, b % 2, k * 256 + o * 128:k * 256 + o * 128 + 128],
                                                  (act_lo if low else act_hi)[:, k * T + g * GW:k * T + (g + 1) * GW],
                                                  start=(k == 0 and w is w_hi and not low), stop=(k == FB - 1 and low == 1))
                                last.then_inc(down_ps, 1)
                        pe.wait_ge(down_ps, n * 24 + (b * 6 + 6))
                        pe.sem_inc(w_used, 1)

            with pe.Fori(0, L) as li:
                ada(li)
                begin(pe, li, 1)
                norm(li, li * 2)
                pairs(0, li)
                out_proj(0, li)
                forget(li)
                pairs(1, li)
                out_proj(1, li)
                pairs(2, li)
                out_proj(2, li)
                begin(pe, li, 9)
                norm(li, li * 2 + 1)
                mlp(li)
            pe.wait_ge(act_done, L * PHASES + PRIME)
            pe.wait_ge(dve_done, L * PHASES + PRIME)
            norm(None, 2 * L)

        @block.scalar
        def _(act):
            own_ = Chain(act, act_self)
            A = nc.scalar.activation
            eps, one, zero = consts[:, 0:1], consts[:, 1:2], consts[:, 2:3]
            act.sem_inc(act_done, PRIME)
            act.sem_inc(mod_rowed, 1)
            for m in range(3):
                act.sem_inc(M[m]["mix_hi_kept"], 1)
                act.sem_inc(M[m]["kv_out"], 1)
            act.sem_inc(M[0]["state_out"], 1)
            for dst, name in CONSTS:
                act.dma_start(dst, I[name]).then_inc(const_in, 16)
            act.wait_ge(const_in, 16 * len(CONSTS))
            A(cond_e[:], cond[:], ACT.Exp, scale=-1.0, bias=zero).then_inc(cond_exp, 1)

            def done():
                own_.restart(settle)
                settle(act)
                act.drain().then_inc(act_done, 1)

            def ada(li):
                begin(act, li, 0)
                for dst, name in LAYER:
                    act.dma_start(dst, from_layer(name, li)).then_inc(layer_in, 16)
                settle(act)
                with act.Fori(0, 12) as q:
                    n = li * 12 + q
                    act.wait_ge(mod_ps, n + 1)
                    act.wait_ge(mod_turned, n + 1)
                    A(mod_row[:], ps[0:2, 0, :], ACT.Copy).then_inc(mod_rowed, 1)
                act.wait_ge(lam_dot, li * 2 + 2)
                A(lam_e[:], lam_s[:], ACT.Exp, bias=zero).then_inc(lam_exp, 1)
                done()

            def squares(c, g):
                for k in range(KB):
                    act.wait_ge(sq_used, c * 24 + (g * KB + k + 1))
                    A(sq[:, k % 2, :], x[:, k * T + g * GW:k * T + (g + 1) * GW], ACT.Square, bias=zero).then_inc(sq_ready, 1)

            def root(c, g):
                act.wait_ge(ms_ready, c * 3 + (g + 1))
                own_.link(A(rb[:, g % 2, :], ps[:, g, 0:GW], ACT.Ln, bias=eps))
                A(rb[:, g % 2, :], rb[:, g % 2, :], ACT.Exp, bias=zero, scale=-0.5).then_inc(rb_ready, 1)

            def norm(li, c, which, p):
                begin(act, li, p)
                shift = 24 * which
                squares(c, 0)
                for g in range(GROUPS):
                    if g + 1 < GROUPS:
                        squares(c, g + 1)
                    if g == 2:
                        act.wait_ge(tn_ready, c * 24 + 8)
                    root(c, g)
                    for k in range(KB):
                        act.wait_ge(tn_ready, c * 24 + (g * KB + k + 1))
                        for a, b, q in segments(g):
                            last = A(h_hi[:, k * T + a:k * T + b], tn[:, k % 2, a - g * GW:b - g * GW], ACT.Identity,
                                     bias=mod[:, shift + k, q:q + 1])
                        last.then_inc(hi_ready, 1)
                done()

            def pairs(m, li):
                s = M[m]
                NC = 2 if m == 2 else 1
                NA = 18 * NC
                scale = [1.0, HD ** -0.5, (HD // 2) ** -0.5][m]
                begin(act, li, [2, 5, 7][m])
                settle(act)
                with act.Fori(0, PAIRS) as j:
                    n = li * PAIRS + j

                    def turned(t):
                        r, c0 = rows(t), 128 * t
                        act.wait_ge(s["turned"], n * 9 + (t + 1))
                        A(qT[:, c0:c0 + r], ps[:, 4 + t % 2, 0:r], ACT.Copy, scale=scale)
                        A(kT[:, c0:c0 + r], ps[:, 4 + t % 2, 128:128 + r], ACT.Copy).then_inc(s["qkT_kept"], 1)

                    for t in range(QT):
                        r = rows(t)
                        act.wait_ge(s["proj"], n * 9 + (t + 1))
                        if t == 0:
                            if m:
                                act.wait_ge(s["kv_out"], n * (STORES[m] * 16) + 1)
                            if m == 0:
                                act.dma_start(decay[:], pair_ap(I["c_decay"], j)).then_inc(s["decay_in"], 16)
                                act.wait_ge(s["state_out"], n * 32 + 1)
                                act.dma_start(states[:, 17, :], pair_ap(I["state"], n)).then_inc(s["state_in"], 16)
                            else:
                                act.dma_start(kT[:, T:NKEY], pair_ap(I["cache_k"][m - 1], n)).then_inc(s["cache_k"], 16)
                                act.dma_start(v_tok[:, 9:11, :], pair_ap(I["cache_v"][m - 1], n)).then_inc(s["cache_v"], 16)
                        A(v_tok[0:r, t, :], ps[0:r, 6 + t % 2, 256:384], ACT.Copy).then_inc(s["v_kept"], 1)
                        if t:
                            turned(t - 1)
                    turned(8)
                    if m:
                        act.wait_ge(s["qkT_kept"], n * 9 + 9)
                        act.dma_start(pair_ap(O["k"][m - 1], n), kT[:, 0:T]).then_inc(s["kv_out"], 16)
                        act.wait_ge(s["v_kept"], n * 9 + 9)
                        act.dma_start(pair_ap(O["v_p"][m - 1], n), v_tok[:, 0:8, :]).then_inc(s["kv_out"], 16)
                        act.dma_start(pair_ap(O["v_s"][m - 1], n), v_tok[0:TS, 8, :]).then_inc(s["kv_out"], 16)
                    if m == 0:
                        act.wait_ge(s["state_kept"], n + 1)
                        act.dma_start(pair_ap(O["state_p"], n), states[:, 16, :]).then_inc(s["state_out"], 16)
                        act.dma_start(pair_ap(O["state_s"], n), states[:, 18, :]).then_inc(s["state_out"], 16)
                    else:
                        gi = [0]

                        def exps(i):
                            t, h = divmod(i, 2)
                            r = rows(t)
                            nk = 128 * (t + 1) if t < 8 else TS + PAST
                            for c in range(NC):
                                a = i * NC + c
                                if m == 1 and i >= 2:
                                    act.wait_ge(s["p_turned"], n * 26 + groups_before(i - 1))
                                if m == 2 and c == 0 and i >= 1:
                                    act.wait_ge(s["p_turned"], n * 26 + groups_before(i))
                                if m == 2 and c == 1 and i >= 1:
                                    act.wait_ge(s["combined"], n * 18 + i)
                                act.wait_ge(s["row_max"], n * NA + (a + 1))
                                A(prob[0:r, a % 2, 0:nk], psf[0:r, 1024 * (a % 2):1024 * (a % 2) + nk], ACT.Exp,
                                  bias=nm[0:r, a % 4:a % 4 + 1], scale=1.0,
                                  accum_out=rs[0:r, a % 4:a % 4 + 1]).then_inc(s["exped"], 1)

                        exps(0)
                        for i in range(18):
                            if i + 1 < 18:
                                exps(i + 1)
                            for q, tiles in enumerate(key_groups(i // 2)):
                                g = gi[0] + q
                                if g % 2 == 1:
                                    keep_turned(act, lambda o, z: A(o, z, ACT.Copy), s, n, i, g, tiles, "pT_odd")
                            gi[0] += len(key_groups(i // 2))
                    if m != 1:
                        act.wait_ge(s["stat"], n + 1)
                        own_.link(A(st2[:], st1[:], ACT.Ln, bias=eps, scale=1.0 / HD))
                        A(st2[:], st2[:], ACT.Exp, bias=zero, scale=-0.5).then_inc(s["rstd"], 1)
                    if m == 0:
                        for g in range(GROUPS):
                            act.wait_ge(s["gate_ps"], n * 3 + (g + 1))
                            A(gate[:, g * GW:(g + 1) * GW], ps[:, g, 0:GW], ACT.Exp, bias=zero,
                              scale=-1.0).then_inc(s["gate_exp"], 1)
                    for i, (bank, c0, w) in enumerate(((4, 0, 512), (5, 512, 512), (3, 1024, 32))):
                        act.wait_ge(s["mix_turned"], n * 3 + (i + 1))
                        settle(act)
                        if m == 0:
                            A(sq_r[:, c0:c0 + w], ps[:, bank, 0:w], ACT.Identity, bias=vec[:, 1, ds(j, 1)],
                              scale=vec[:, 0, ds(j, 1)]).then_inc(s["y_pre"], 1)
                            act.wait_ge(s["y_gated"], n * 3 + (i + 1))
                            A(mix_hi[:, ds(j * T + c0, w)], sq_r[:, c0:c0 + w], ACT.Copy).then_inc(s["mix_hi_kept"], 1)
                        elif m == 1:
                            A(mix_hi[:, ds(j * T + c0, w)], ps[:, bank, 0:w], ACT.Copy).then_inc(s["mix_hi_kept"], 1)
                        else:
                            A(mix_hi[:, ds(j * T + c0, w)], ps[:, bank, 0:w], ACT.Identity, bias=zero,
                              scale=vec[:, 2, ds(j, 1)]).then_inc(s["mix_hi_kept"], 1)
                    own_.restart(settle)
                if m:
                    act.wait_ge(s["kv_out"], (li + 1) * (PAIRS * STORES[m] * 16) + 1)
                else:
                    act.wait_ge(s["state_out"], (li + 1) * (PAIRS * 32) + 1)
                done()

            def forget(li):
                begin(act, li, 4)
                act.wait_ge(layer_in, (li + 1) * 16 * len(LAYER))
                act.dma_start(wf_raw[:], from_layer("w_forget", li)).then_inc(f_in, 16)
                act.dma_start(tri[:], I["c_tri"]).then_inc(f_in, 16)
                act.dma_start(lf_tok[:, 9:11, :], from_layer("cache_logf", li)).then_inc(f_in, 16)
                act.wait_ge(f_z, li + 1)
                own_.link(A(fe[:], fe[:], ACT.Exp, bias=zero[0:6], scale=-1.0))
                A(fe[:], fe[:], ACT.Ln, bias=one[0:6]).then_inc(f_ln, 1)
                act.wait_ge(f_log, li + 1)
                act.dma_start(from_layer2(O["logf"], li), fz[:]).then_inc(f_out, 16)
                act.wait_ge(f_out, (li + 1) * 16)
                done()

            def from_layer2(a, li):
                return a[ds(li, 1)].rearrange("o p c -> (o p) c")

            def mlp(li):
                begin(act, li, 10)
                settle(act)
                with act.Fori(0, MLP_CHUNKS) as f:
                    n = li * MLP_CHUNKS + f
                    for b in range(FB):
                        for g in range(GROUPS):
                            i = b * 3 + g
                            act.wait_ge(up_ps, n * 12 + (i + 1))
                            if i >= 2:
                                act.wait_ge(sq_kept, n * 12 + (i - 1))
                            else:
                                act.wait_ge(up_lo, n * 12 + 1)
                            A(relu_b[:, i % 2, :], ps[:, i % 6, 0:GW], ACT.Relu, bias=zero).then_inc(up_relu, 1)
                            act.wait_ge(up_relu, n * 12 + (i + 1))
                            A(act_hi[:, b * T + g * GW:b * T + (g + 1) * GW], relu_b[:, i % 2, :], ACT.Square,
                              bias=zero).then_inc(up_hi, 1)
                done()

            def plain(li, p):
                begin(act, li, p)
                done()

            with act.Fori(0, L) as li:
                ada(li)
                norm(li, li * 2, 0, 1)
                pairs(0, li)
                plain(li, 3)
                forget(li)
                pairs(1, li)
                plain(li, 6)
                pairs(2, li)
                plain(li, 8)
                norm(li, li * 2 + 1, 1, 9)
                mlp(li)
            act.wait_ge(dve_done, L * PHASES + PRIME)
            c = 2 * L
            for g in range(GROUPS):
                squares(c, g)
                if g == 2:
                    act.wait_ge(y_ready, 8)
                root(c, g)
            for k in range(KB):
                act.wait_ge(y_ready, 2 * KB + k + 1)
                act.dma_start(O["y"][:, k, :], x[:, k * T:(k + 1) * T]).then_inc(y_out, 16)
            act.wait_ge(y_out, 16 * KB)
            for m in range(3):
                if m:
                    act.wait_ge(M[m]["kv_out"], L * PAIRS * STORES[m] * 16 + 1)
            act.wait_ge(M[0]["state_out"], L * PAIRS * 32 + 1)
            act.wait_ge(f_out, L * 16)

        @block.vector
        def _(dve):
            v = nc.vector
            own_ = Chain(dve, dve_self)
            link = own_.link
            dve.sem_inc(dve_done, PRIME)
            dve.sem_inc(mod_kept, 1)
            dve.sem_inc(out_kept, 6)
            dve.sem_inc(down_kept, 6)
            dve.sem_inc(up_lo, 1)
            for m in range(3):
                dve.sem_inc(M[m]["mix_lo_kept"], 1)
            dve.wait_ge(cond_exp, 1)
            link(v.tensor_scalar(cond_e[:], cond_e[:], 1.0, None, ALU.add))
            link(v.reciprocal(cond_e[:], cond_e[:]))
            v.tensor_tensor(cond[:], cond[:], cond_e[:], ALU.mult).then_inc(cond_ready, 1)
            own_.restart(settle)

            def done():
                own_.restart(settle)
                settle(dve)
                dve.drain().then_inc(dve_done, 1)

            def ada(li):
                begin(dve, li, 0)
                dve.wait_ge(layer_in, (li + 1) * 16 * len(LAYER))
                for i in range(2):
                    v.tensor_tensor_reduce(lam_p[:], lam_v[:, 2 * i, :], lam_v[:, 2 * i + 1, :], 1.0, 0.0, ALU.mult,
                                           ALU.add, lam_s[:, i:i + 1]).then_inc(lam_dot, 1)
                    dve.wait_ge(lam_dot, li * 2 + (i + 1))
                settle(dve)
                with dve.Fori(0, 12) as q:
                    n = li * 12 + q
                    dve.wait_ge(mod_turned, n + 2)
                    v.tensor_tensor(mod[:, ds(q * 4, 4), :], ps[:, 1, 0:8].rearrange("p (b s) -> p b s", b=4),
                                    ada_bias[:, ds(q * 4, 4)].unsqueeze(2).to_broadcast([128, 4, 2]),
                                    ALU.add).then_inc(mod_kept, 1)
                dve.wait_ge(mod_kept, li * 12 + 13)
                for w in range(2):
                    own_.mark(v.scalar_tensor_tensor(scale_in[:, w, :, :], mod[:, 24 * w + 8:24 * w + 16, :], 1.0,
                                                     norm_g[:, w, :].unsqueeze(2).to_broadcast([128, KB, 2]),
                                                     ALU.add, ALU.mult))
                own_.mark(v.tensor_scalar(vec[:, 2, :], vec[:, 2, :], lam_c[:, 1:2], None, ALU.mult))
                dve.wait_ge(lam_exp, li + 1)
                link(v.tensor_tensor(lam_n[:], lam_e[:, 1:2], lam_e[:, 0:1], ALU.subtract))
                link(v.tensor_tensor(lam_n[:], lam_n[:], lam_c[:, 0:1], ALU.subtract))
                done()

            def norm(li, c, which, p):
                begin(dve, li, p)
                shift = 24 * which

                def scaled(i):
                    g, k = divmod(i, KB)
                    if k == 0:
                        dve.wait_ge(rb_ready, c * 3 + (g + 1))
                    if i >= 2:
                        dve.wait_ge(hi_ready, c * 24 + (i - 1))
                        dve.wait_ge(lo_ready, c * 24 + (i - 1))
                    for a, b, q in segments(g):
                        last = v.scalar_tensor_tensor(tn[:, k % 2, a - g * GW:b - g * GW], x[:, k * T + a:k * T + b],
                                                      scale_in[:, which, k, q:q + 1], rb[:, g % 2, a - g * GW:b - g * GW],
                                                      ALU.mult, ALU.mult)
                    last.then_inc(tn_ready, 1)

                scaled(0)
                for i in range(24):
                    g, k = divmod(i, KB)
                    if i + 1 < 24:
                        scaled(i + 1)
                    dve.wait_ge(hi_ready, c * 24 + (i + 1))
                    for a, b, q in segments(g):
                        last = v.scalar_tensor_tensor(h_lo[:, k * T + a:k * T + b], tn[:, k % 2, a - g * GW:b - g * GW],
                                                      mod[:, shift + k, q:q + 1], h_hi[:, k * T + a:k * T + b].bitcast(F32),
                                                      ALU.add, ALU.subtract)
                    last.then_inc(lo_ready, 1)
                dve.wait_ge(lo_ready, c * 24 + 24)
                done()

            def rotate(m, t, bank):
                half = 32 if m == 0 else 16
                r = rows(t)
                tab = rope_r if m == 0 else rope_d
                tmp = rope_r_tmp if m == 0 else rope_d_tmp
                G = 256 // (2 * half)
                src = ps[0:r, bank, 0:256].rearrange("p (g s d) -> p g s d", g=G, s=2)
                dst = qk_tok[0:r, t % 2, :].rearrange("p (g s d) -> p g s d", g=G, s=2)
                both = tmp[0:r, 0:256].rearrange("p (g s d) -> p g s d", g=G, s=2)
                t2 = tmp[0:r, 256:384].rearrange("p (g d) -> p g d", g=G)
                t1 = tmp[0:r, 384:512].rearrange("p (g d) -> p g d", g=G)
                cos = tab[0:r, t, 0, :].unsqueeze(1).to_broadcast([r, G, half])
                sin = tab[0:r, t, 1, :].unsqueeze(1).to_broadcast([r, G, half])
                own_.mark(v.tensor_tensor(both[:, :, 0, :], src[:, :, 0, :], cos, ALU.mult))
                own_.mark(v.tensor_tensor(both[:, :, 1, :], src[:, :, 1, :], cos, ALU.mult))
                own_.mark(v.tensor_tensor(t2, src[:, :, 1, :], sin, ALU.mult))
                link(v.tensor_tensor(t1, src[:, :, 0, :], sin, ALU.mult))
                own_.mark(v.tensor_tensor(dst[:, :, 0, :], both[:, :, 0, :], t2, ALU.subtract))
                return v.tensor_tensor(dst[:, :, 1, :], both[:, :, 1, :], t1, ALU.add)

            def pairs(m, li):
                s = M[m]
                NC = 2 if m == 2 else 1
                NA = 18 * NC
                begin(dve, li, [2, 5, 7][m])
                own_.mark(v.memset(o_tok[:, 8, :], 0.0))
                if m == 0:
                    own_.mark(v.memset(states[:, 0, :], 0.0))
                own_.restart(settle)
                settle(dve)
                with dve.Fori(0, PAIRS) as j:
                    n = li * PAIRS + j
                    if m == 1:
                        v.tensor_copy(sel_pair[:], sel[:, ds(j * 2, 2), :]).then_inc(s["sel_kept"], 1)
                    for t in range(QT):
                        r = rows(t)
                        dve.wait_ge(s["proj"], n * 9 + (t + 1))
                        dve.wait_ge(s["v_kept"], n * 9 + (t + 1))
                        if m == 1:
                            v.tensor_copy(qk_tok[0:r, t % 2, :], ps[0:r, 6 + t % 2, 0:256]).then_inc(s["qk_kept"], 1)
                        else:
                            last = rotate(m, t, 6 + t % 2)
                            if m == 2:
                                last.then_inc(s["qk_kept"], 1)
                                dve.wait_ge(s["qk_kept"], n * 9 + (t + 1))
                            else:
                                link(last)
                                for h in range(2):
                                    last = v.tensor_scalar(o_tok[0:r, t, 64 * h:64 * h + 64],
                                                           qk_tok[0:r, t % 2, 128 + 64 * h:192 + 64 * h],
                                                           kw_t[0:r, t // 8, ds(j * 2 + h, 1)], None, ALU.mult)
                                last.then_inc(s["qk_kept"], 1)
                    if m == 0:
                        retention(s, n, j)
                    else:
                        attention(m, s, n, NC, NA)
                    post(m, s, n, j)
                    own_.restart(settle)
                done()

            def retention(s, n, j):
                dve.wait_ge(s["u_ps"], n + 1)
                dve.wait_ge(s["state_in"], (n + 1) * 16)
                dve.wait_ge(s["decay_in"], (n + 1) * 16)
                dve.wait_ge(s["state_out"], n * 32 + 1)
                own_.mark(v.scalar_tensor_tensor(states[:, 18, :], states[:, 17, :], cd_t[:, 1, ds(j, 1)], ps[:, 2, 0:64],
                                                 ALU.mult, ALU.add))
                for c in range(16):
                    last = v.scalar_tensor_tensor(states[:, c + 1, :], states[:, c, :], cd_t[:, 0, ds(j, 1)],
                                                  ps[:, c % 2, 64 * (c // 2):64 * (c // 2) + 64], ALU.mult, ALU.add)
                    if c < 15:
                        link(last)
                last.then_inc(s["state_kept"], 1)

                def decayed(i):
                    t, h = divmod(i, 2)
                    r = rows(t)
                    dve.wait_ge(s["s_ps"], n * 18 + (i + 1))
                    if i >= 2:
                        dve.wait_ge(s["o_ps"], n * 18 + (i - 1))
                    v.tensor_tensor(s_mix[0:r, i % 2, 0:r], ps[0:r, 4 + i % 2, 0:r], decay[0:r, h, 0:r],
                                    ALU.mult).then_inc(s["s_kept"], 1)

                decayed(0)
                for i in range(18):
                    t, h = divmod(i, 2)
                    r = rows(t)
                    if i + 1 < 18:
                        decayed(i + 1)
                    dve.wait_ge(s["o_ps"], n * 18 + (i + 1))
                    v.tensor_scalar(o_tok[0:r, t, 64 * h:64 * h + 64], ps[0:r, 6 + i % 2, 0:64],
                                    qw_t[0:r, ds(j * 2 + h, 1)], None, ALU.mult).then_inc(s["o_kept"], 1)

            def attention(m, s, n, NC, NA):
                gi = [0]

                def maxima(i):
                    t, h = divmod(i, 2)
                    r = rows(t)
                    nk = 128 * (t + 1) if t < 8 else TS + PAST
                    for c in range(NC):
                        a = i * NC + c
                        dve.wait_ge(s["score"], n * NA + (a + 1))
                        v.tensor_reduce(nm[0:r, a % 4:a % 4 + 1], psf[0:r, 1024 * (a % 2):1024 * (a % 2) + nk], AX.X,
                                        ALU.max, negate=True).then_inc(s["row_max"], 1)

                maxima(0)
                for i in range(18):
                    t, h = divmod(i, 2)
                    r = rows(t)
                    nk = 128 * (t + 1) if t < 8 else TS + PAST
                    if i + 1 < 18 and m == 1:
                        maxima(i + 1)
                    if m == 1:
                        dve.wait_ge(s["exped"], n * NA + (i + 1))
                        inv = own_.mark(v.reciprocal(ri[0:r, i % 2:i % 2 + 1], rs[0:r, i % 4:i % 4 + 1]))
                    else:
                        a0, a1 = (2 * i) % 4, (2 * i + 1) % 4
                        dve.wait_ge(s["exped"], n * NA + (2 * i + 2))
                        inv = own_.mark(v.reciprocal(ri[0:r, i % 2:i % 2 + 1], rs[0:r, a0:a0 + 1]))
                        link(v.reciprocal(coef[0:r], rs[0:r, a1:a1 + 1]))
                        link(v.tensor_scalar(coef[0:r], coef[0:r], rs[0:r, a0:a0 + 1], lam_n[0:r], ALU.mult, ALU.mult))
                        v.scalar_tensor_tensor(prob[0:r, 0, 0:nk], prob[0:r, 1, 0:nk], coef[0:r], prob[0:r, 0, 0:nk],
                                               ALU.mult, ALU.add).then_inc(s["combined"], 1)
                        if i + 1 < 18:
                            maxima(i + 1)
                    groups = key_groups(t)
                    for q, tiles in enumerate(groups):
                        g = gi[0] + q
                        if g % 2 == 0:
                            keep_turned(dve, lambda o, z: v.tensor_copy(o, z), s, n, i, g, tiles, "pT_even")
                    gi[0] += len(groups)
                    dve.wait_ge(s["pv"], n * 26 + gi[0])
                    own_.wait(inv)
                    v.tensor_scalar(o_tok[0:r, t, 64 * h:64 * h + 64], ps[0:r, 6 + i % 2, 0:64], ri[0:r, i % 2:i % 2 + 1],
                                    None, ALU.mult).then_inc(s["o_kept"], 1)

            def post(m, s, n, j):
                dve.wait_ge(s["o_kept"], n * 18 + 18)
                o = o_tok[:].rearrange("p t (h d) -> p (t h) d", h=2)
                sqs = (sq_r if m == 0 else sq_d)[:].rearrange("p (a d) -> p a d", d=64)
                if m == 1:
                    settle(dve)
                    dve.drain().then_inc(s["normed"], 1)
                else:
                    if m == 0:
                        link(v.tensor_reduce(st3[:], o, AX.X, ALU.add))
                        link(v.tensor_scalar(st3[:], st3[:], 1.0 / HD, None, ALU.mult))
                        link(v.tensor_tensor(o, o, st3[:].unsqueeze(2).to_broadcast([128, 18, 64]), ALU.subtract))
                    link(v.tensor_tensor(sqs, o, o, ALU.mult))
                    v.tensor_reduce(st1[:], sqs, AX.X, ALU.add).then_inc(s["stat"], 1)
                    dve.wait_ge(s["rstd"], n + 1)
                    v.tensor_tensor(o, o, st2[:].unsqueeze(2).to_broadcast([128, 18, 64]), ALU.mult).then_inc(s["normed"], 1)
                if m == 0:
                    for g in range(GROUPS):
                        z = gate[:, g * GW:(g + 1) * GW]
                        dve.wait_ge(s["gate_exp"], n * 3 + (g + 1))
                        link(v.tensor_scalar(z, z, 1.0, None, ALU.add))
                        link(v.reciprocal(z, z))
                        link(v.tensor_tensor(z, z, ps[:, g, 0:GW], ALU.mult))
                for i, (bank, c0, w) in enumerate(((4, 0, 512), (5, 512, 512), (3, 1024, 32))):
                    lo = mix_lo[:, ds(j * T + c0, w)]
                    hi = mix_hi[:, ds(j * T + c0, w)].bitcast(F32)
                    if m == 0:
                        y = sq_r[:, c0:c0 + w]
                        dve.wait_ge(s["y_pre"], n * 3 + (i + 1))
                        v.tensor_tensor(y, y, gate[:, c0:c0 + w], ALU.mult).then_inc(s["y_gated"], 1)
                        dve.wait_ge(s["mix_hi_kept"], n * 3 + (i + 2))
                        v.tensor_tensor(lo, y, hi, ALU.subtract).then_inc(s["mix_lo_kept"], 1)
                    else:
                        dve.wait_ge(s["mix_hi_kept"], n * 3 + (i + 2))
                        g = 1.0 if m == 1 else vec[:, 2, ds(j, 1)]
                        v.scalar_tensor_tensor(lo, ps[:, bank, 0:w], g, hi, ALU.mult, ALU.subtract).then_inc(
                            s["mix_lo_kept"], 1)

            def residual(i, o, g, gain, out_sem):
                for a, b, q in segments(g):
                    xs = x[:, o + a:o + b] if isinstance(o, int) else x[:, ds(o + a, b - a)]
                    gs = gain(q)
                    last = v.scalar_tensor_tensor(xs, ps[:, i % 6, a - g * GW:b - g * GW], gs, xs, ALU.mult, ALU.add)
                last.then_inc(out_sem, 1)

            def out_proj(m, li):
                begin(dve, li, [3, 6, 8][m])
                c = li * 3 + m
                settle(dve)
                with dve.Fori(0, 2) as r:
                    for i in range(12):
                        dve.wait_ge(out_ps, c * 24 + r * 12 + (i + 1))
                        b, g = divmod(i, 3)
                        residual(i, r * (4 * T) + b * T, g, lambda q: mod[:, ds(r * 4 + (16 + b), 1), q], out_kept)
                done()

            def forget(li):
                begin(dve, li, 4)
                dve.wait_ge(f_in, (li + 1) * 48)
                link(v.tensor_copy(wf_hi[:], wf_raw[:]))
                v.tensor_tensor(wf_lo[:], wf_raw[:], wf_hi[:].bitcast(F32), ALU.subtract).then_inc(f_wsplit, 1)
                own_.mark(v.memset(cum_bf[:], 0.0))
                dve.wait_ge(f_ps, li + 1)
                for g in range(GROUPS):
                    last = own_.mark(v.tensor_scalar(fz[:, g * GW:(g + 1) * GW], ps[0:6, g, 0:GW], bias_f[:], None, ALU.add))
                own_.wait(last)
                v.scalar_tensor_tensor(fe[:], fz[:], -1.0, fz[:], ALU.mult, ALU.max).then_inc(f_z, 1)
                dve.wait_ge(f_z, li + 1)
                link(v.tensor_scalar(fz[:], fz[:], 0.0, None, ALU.min))
                dve.wait_ge(f_ln, li + 1)
                v.tensor_tensor(fz[:], fz[:], fe[:], ALU.subtract).then_inc(f_log, 1)
                dve.wait_ge(f_turned, li + 1)
                for t in range(QT):
                    r = rows(t)
                    last = v.tensor_copy(lf_tok[0:r, t, :], ps[0:r, 3, 8 * t:8 * t + 6])
                last.then_inc(f_tok, 1)
                dve.wait_ge(f_cum, li + 1)
                own_.mark(v.tensor_copy(cum[:, 0:TP], psf[0:6, 4 * 512:4 * 512 + TP]))
                own_.mark(v.tensor_copy(cum[:, TP:T], ps[0:6, 6, PAST:PAST + TS]))
                link(v.tensor_copy(cum[:, T:NKEY], ps[0:6, 6, 0:PAST]))
                link(v.tensor_copy(cum_bf[0:6, :], cum[:]))
                link(v.tensor_tensor(cum[:], cum[:], cum_bf[0:6, :], ALU.subtract))
                own_.mark(v.tensor_copy(cum_bf[32:38, :], cum[:]))
                link(v.tensor_copy(cum_mid[:], cum[:]))
                link(v.tensor_tensor(cum_bf[64:70, :], cum[:], cum_mid[:], ALU.subtract))
                done()

            def mlp(li):
                begin(dve, li, 10)
                settle(dve)
                with dve.Fori(0, MLP_CHUNKS) as f:
                    n = li * MLP_CHUNKS + f
                    for b in range(FB):
                        for g in range(GROUPS):
                            i = b * 3 + g
                            dve.wait_ge(up_relu, n * 12 + (i + 1))
                            v.tensor_tensor(sq_b[:, i % 2, :], relu_b[:, i % 2, :], relu_b[:, i % 2, :],
                                            ALU.mult).then_inc(sq_kept, 1)
                            dve.wait_ge(sq_kept, n * 12 + (i + 1))
                            dve.wait_ge(up_hi, n * 12 + (i + 1))
                            c0 = b * T + g * GW
                            v.tensor_tensor(act_lo[:, c0:c0 + GW], sq_b[:, i % 2, :], act_hi[:, c0:c0 + GW].bitcast(F32),
                                            ALU.subtract).then_inc(up_lo, 1)
                    dve.wait_ge(up_lo, n * 12 + 13)
                    for i in range(24):
                        dve.wait_ge(down_ps, n * 24 + (i + 1))
                        b, g = divmod(i, 3)
                        residual(i, b * T, g, lambda q: mod[:, 40 + b, q:q + 1], down_kept)
                    dve.wait_ge(down_kept, n * 24 + 30)
                done()

            with dve.Fori(0, L) as li:
                ada(li)
                norm(li, li * 2, 0, 1)
                pairs(0, li)
                out_proj(0, li)
                forget(li)
                pairs(1, li)
                out_proj(1, li)
                pairs(2, li)
                out_proj(2, li)
                norm(li, li * 2 + 1, 1, 9)
                mlp(li)
            dve.wait_ge(act_done, L * PHASES + PRIME)
            for g in range(GROUPS):
                dve.wait_ge(rb_ready, 2 * L * 3 + g + 1)
                for k in range(KB):
                    xs = x[:, k * T + g * GW:k * T + (g + 1) * GW]
                    v.scalar_tensor_tensor(xs, xs, final_g[:, k:k + 1], rb[:, g % 2, :], ALU.mult, ALU.mult).then_inc(
                        y_ready, 1)


STORES = [0, 3, 3]


def groups_before(i):
    return sum(len(key_groups(u // 2)) for u in range(i))


def tables():
    f = np.float32
    pos = np.concatenate([np.arange(TP), PAST + np.arange(TS), np.zeros(96)]).astype(f)

    def rope(half):
        inv = f(10000.0) ** (-np.arange(half, dtype=f) / f(half))
        ang = pos[:, None] * inv[None, :]
        both = np.stack([np.cos(ang), np.sin(ang)], 1).astype(f)
        return np.ascontiguousarray(both.reshape(QT, 128, 2, half).transpose(1, 0, 2, 3))

    g = 1.0 - 2.0 ** (-5.0 - np.arange(6, dtype=np.float64))
    p = np.arange(128)
    kw = np.zeros((128, 2, 6))
    kw[:, 0] = g[None] ** (CHUNK - 1.0 - (p % CHUNK))[:, None] * HD ** -0.5
    kw[:, 1] = g[None] ** (TS - 1.0 - (p % TS))[:, None] * HD ** -0.5
    qw = g[None] ** (p % CHUNK + 1.0)[:, None]
    head = 2 * np.arange(3)[None, :] + (p // 64)[:, None]
    cd = np.stack([g[head] ** CHUNK, g[head] ** TS], 1)
    same = (p[:, None] // CHUNK) == (p[None, :] // CHUNK)
    decay = np.where(same, g[:, None, None] ** np.abs(p[:, None] - p[None, :]) * HD ** -0.5, 0.0) / qw.T[:, None, :]
    decay = decay.reshape(3, 2, 128, 128).transpose(0, 2, 1, 3)
    sel = np.zeros((128, 6, 128))
    for h in range(6):
        sel[[h, 32 + h, 64 + h], h, :] = -1.0
    mask = np.zeros((128, 2, 128))
    mask[:, 0] = np.where(p[None, :] > p[:, None], NEG, 0.0)
    mask[:, 1] = np.where((p[None, :] >= 64) & (p[:, None] < 64), NEG, 0.0)
    tri = np.concatenate([(p[:, None] <= p[None, :]), np.ones((128, 512))], 1)
    consts = np.tile(np.array([[EPS, 1.0, 0.0, 0.0]]), (128, 1))
    lam = np.array([0.8 - 0.6 * np.exp(-0.3 * li) for li in range(L)])
    c_lam = np.tile(np.stack([lam, 1.0 - lam], 1)[:, None, :], (1, 128, 1))
    bf = np.dtype("bfloat16")
    t = {"c_ident": np.eye(128), "c_mean": np.full((128, 128), 1.0 / D), "c_kw": kw, "c_qw": qw, "c_cd": cd,
         "c_decay": decay, "c_tri": tri, "c_consts": consts, "c_lam": c_lam}
    t = {k: np.ascontiguousarray(a, dtype=f) for k, a in t.items()}
    t.update(c_rope_r=rope(32), c_rope_d=rope(16), c_ident_bf=np.eye(128).astype(bf), c_mask=mask.astype(bf),
             c_sel=sel.astype(bf))
    return t


def laid_out(i):
    i = {k: np.asarray(a) for k, a in i.items()}
    c = np.ascontiguousarray

    def blocks(a):
        return c(a.reshape(L, -1, 128).transpose(0, 2, 1))

    def unit(w, width):
        k, n = w.shape[1] // 128, w.shape[2] // width
        return w.reshape(L, k, 128, n, width).transpose(0, 3, 2, 1, 4).reshape(L, n, 128, k * width)

    a = {}
    xs = np.concatenate([i["x_prompt"][0], i["x_sample"][0]], 0)
    a["x"] = c(xs.reshape(T, KB, 128).transpose(2, 1, 0).reshape(128, KB * T))
    cc = np.concatenate([i["c_prompt"], i["c_sample"]], 0)
    a["c"] = c(cc.reshape(2, KB, 128).transpose(2, 1, 0))
    ada = i["w_ada"].reshape(L, 4, 2, 128, 12, 512).transpose(0, 4, 1, 3, 2, 5)
    a["w_ada"] = c(ada.reshape(L * 48, 128, UNIT))
    w = unit(i["w_in"][:, :, :4 * 384 + 3 * 384], 128)
    wd = unit(i["w_in"][:, :, 7 * 384 + 6:], 128)
    out = i["w_out"].reshape(L, 3, 384, D)
    outs = [np.concatenate([unit(out[:, m], 256), np.zeros((L, 4, 128, 256), np.float32)], 3) for m in range(3)]
    order = [w[:, [j, 3 + j, 6 + j, 9 + j]] for j in range(3)] + [outs[0]]
    order += [w[:, [12 + j, 15 + j, 18 + j]] for j in range(3)] + [outs[1]]
    order += [wd[:, [j, 3 + j, 6 + j]] for j in range(3)] + [outs[2]]
    up = unit(i["w_up"], 128).reshape(L, MLP_CHUNKS, 4, 128, UNIT)
    down = i["w_down"].reshape(L * MLP_CHUNKS, FB, 128, 4, 256).transpose(0, 3, 2, 1, 4)
    down = down.reshape(L, MLP_CHUNKS, 4, 128, UNIT)
    order += [np.concatenate([up, down], 2).reshape(L, 8 * MLP_CHUNKS, 128, UNIT)]
    a["w"] = c(np.concatenate(order, 1).reshape(L * NU, 128, UNIT))
    wf = i["w_in"][:, :, 7 * 384:7 * 384 + 6].reshape(L, KB, 128, 6).transpose(0, 2, 1, 3).reshape(L, 128, 48)
    a["w_forget"] = c(np.concatenate([wf, np.zeros((L, 128, 128), np.float32)], 2))
    a["b_ada"] = blocks(i["b_ada"])
    a["norm_g"] = c(np.stack([blocks(i["norm1_g"]), blocks(i["norm2_g"])], 2))
    a["final_g"] = c(i["final_g"].reshape(KB, 128).T)
    a["vec"] = c(np.stack([blocks(i[n]) for n in ("ret_norm_g", "ret_norm_b", "diff_norm_g")], 2))
    a["b_forget"] = c(i["b_forget"][:, :, None])
    lam = np.stack([i[n] for n in ("lam_q1", "lam_k1", "lam_q2", "lam_k2")], 1)
    a["lam"] = c(np.broadcast_to(lam[:, None], (L, 128, 4, 32)))
    for m, n in enumerate(("fox", "diff")):
        k = i[f"cache_{n}_k"][:, 0].reshape(L, PAST, 3, 128).transpose(0, 2, 3, 1)
        v = i[f"cache_{n}_v"][:, 0].reshape(L, 2, 128, 3, 128).transpose(0, 3, 2, 1, 4)
        a[f"cache_k{m}"] = c(k.reshape(L * 3, 128, PAST))
        a[f"cache_v{m}"] = c(v.reshape(L * 3, 128, 2, 128))
    a["cache_logf"] = c(i["cache_fox_logf"][:, 0].reshape(L, 2, 128, 6).transpose(0, 2, 1, 3))
    a["state"] = c(i["state_ret"].reshape(L * 3, 128, HD))
    return a


OUTPUTS = {"y": (128, KB, T), "k0": (L * 3, 128, T), "k1": (L * 3, 128, T), "v_p0": (L * 3, 128, 8, 128),
           "v_p1": (L * 3, 128, 8, 128), "v_s0": (L * 3, TS, 128), "v_s1": (L * 3, TS, 128), "logf": (L, 6, T),
           "state_p": (L * 3, 128, HD), "state_s": (L * 3, 128, HD)}


def kernel(**inputs):
    import concourse.bacc as bacc
    from concourse.bass_utils import run_bass_kernel_spmd

    nc = bacc.Bacc("TRN2", target_bir_lowering=False, num_devices=1)
    arrays = {**laid_out(inputs), **tables()}
    I = {n: nc.dram_tensor(f"in_{n}", a.shape, mybir.dt.from_np(a.dtype), kind="ExternalInput").ap()
         for n, a in arrays.items()}
    O = {n: nc.dram_tensor(f"out_{n}", s, mybir.dt.float32, kind="ExternalOutput").ap() for n, s in OUTPUTS.items()}
    for n in ("cache_k", "cache_v"):
        I[n] = [I[n + "0"], I[n + "1"]]
    for n in ("k", "v_p", "v_s"):
        O[n] = [O[n + "0"], O[n + "1"]]
    build(nc, I, O)
    r = run_bass_kernel_spmd(nc, [{f"in_{n}": a for n, a in arrays.items()}], core_ids=[0]).results[0]
    r = {n: np.asarray(r[f"out_{n}"]) for n in OUTPUTS}
    y = r["y"].transpose(2, 1, 0).reshape(T, D)
    parts = []
    for m in range(2):
        k = r[f"k{m}"].reshape(L, 3, 128, T).transpose(0, 3, 1, 2).reshape(L, T, 6, HD)
        vp = r[f"v_p{m}"].reshape(L, 3, 128, 8, 128).transpose(0, 3, 2, 1, 4).reshape(L, 1, TP, 6, HD)
        vs = r[f"v_s{m}"].reshape(L, 3, TS, 128).transpose(0, 2, 1, 3).reshape(L, 1, TS, 6, HD)
        parts.append((k[:, None, :TP], vp, k[:, None, TP:], vs))
    logf = r["logf"].transpose(0, 2, 1)
    sp, ss = (r[n].reshape(L, 1, 6, HD, HD) for n in ("state_p", "state_s"))
    (fkp, fvp, fks, fvs), (dkp, dvp, dks, dvs) = parts
    c = np.ascontiguousarray
    return tuple(c(z) for z in (y[None, :TP], y[None, TP:], fkp, fvp, logf[:, None, :TP], dkp, dvp, sp,
                                fks, fvs, logf[:, None, TP:], dks, dvs, ss))
```
